# Optimizing a Trainium2 kernel written in Bass

```python
import math
import jax, jax.numpy as jnp
from jax import lax
import numpy as np

D_MODEL = 2048
BATCH = 1
SEQ = 256
DEPTH = 1

HEAD_DIM = 128
N_HEADS_FOX = 8
N_HEADS_DIL = 8
D_FOX = N_HEADS_FOX * HEAD_DIM
D_DIL = N_HEADS_DIL * HEAD_DIM
MIX_WIDTH = D_FOX + D_DIL
D_IN_PROJ = 3 * D_FOX + N_HEADS_FOX + 3 * D_DIL
D_FF = 256 * (-(-8 * D_MODEL // (3 * 256)))
PLE_DIM = 256
Q_BLOCK = 128
DILATED_PATTERNS = ((128, 1), (512, 4), (2048, 16))
N_REL_BUCKETS = 32
REL_MAX_DISTANCE = 2048
RMS_EPS = 1e-6
NEG_INF = -1e30

kernel_name = "hybrid_fox_dilated_macaron_block"

def rmsnorm(x, g):
    xf = x.astype(jnp.float32)
    y = xf * lax.rsqrt(jnp.mean(xf * xf, axis=-1, keepdims=True) + RMS_EPS)
    return (y * g.astype(jnp.float32)).astype(x.dtype)

def swiglu(h, w_gate, w_up, w_down):
    return (jax.nn.silu(h @ w_gate) * (h @ w_up)) @ w_down

def t5_bucket(dist):
    max_exact = N_REL_BUCKETS // 2
    d = jnp.maximum(dist, 1).astype(jnp.float32)
    large = max_exact + (jnp.log(d / max_exact) / math.log(REL_MAX_DISTANCE / max_exact)
                         * (N_REL_BUCKETS - max_exact)).astype(jnp.int32)
    large = jnp.minimum(large, N_REL_BUCKETS - 1)
    return jnp.where(dist < max_exact, dist, large)

def forgetting_attention(q, k, v, log_f):
    B, S, H, Dh = q.shape
    scale = HEAD_DIM ** -0.5
    c = jnp.cumsum(log_f, axis=1).transpose(0, 2, 1)
    outs = []
    for i in range(S // Q_BLOCK):
        t0, t1 = i * Q_BLOCK, (i + 1) * Q_BLOCK
        s = jnp.einsum('bqhd,bkhd->bhqk', q[:, t0:t1], k[:, :t1]).astype(jnp.float32) * scale
        decay = c[:, :, t0:t1, None] - c[:, :, None, :t1]
        causal = (t0 + jnp.arange(Q_BLOCK))[:, None] >= jnp.arange(t1)[None, :]
        s = jnp.where(causal, s + decay, NEG_INF)
        pr = jax.nn.softmax(s, axis=-1)
        outs.append(jnp.einsum('bhqk,bkhd->bqhd', pr.astype(v.dtype), v[:, :t1]))
    return jnp.concatenate(outs, axis=1)

def dilated_window_attention(q, k, v, rel_table, window, dilation):
    B, S, H, Dh = q.shape
    n = window // dilation
    blk = n
    L = S // dilation
    nb = -(-L // blk)
    Lp = nb * blk
    scale = HEAD_DIM ** -0.5

    def sub(a):
        return a.reshape(B, L, dilation, H, Dh).transpose(0, 2, 1, 3, 4)

    qs = jnp.pad(sub(q), ((0, 0), (0, 0), (0, Lp - L), (0, 0), (0, 0)))
    kv_pad = ((0, 0), (0, 0), (blk, Lp - L), (0, 0), (0, 0))
    ks = jnp.pad(sub(k), kv_pad)
    vs = jnp.pad(sub(v), kv_pad)

    def windows(a):
        prev = a[:, :, :Lp].reshape(B, dilation, nb, blk, H, Dh)
        cur = a[:, :, blk:].reshape(B, dilation, nb, blk, H, Dh)
        return jnp.concatenate([prev, cur], axis=3)

    qb = qs.reshape(B, dilation, nb, blk, H, Dh)
    kw, vw = windows(ks), windows(vs)

    qi = jnp.arange(blk)[:, None]
    ki = jnp.arange(2 * blk)[None, :]
    rel = qi + blk - ki
    key_sub = (jnp.arange(nb) * blk)[:, None, None] - blk + ki[None]
    valid = (rel >= 0)[None] & (rel <= n)[None] & (key_sub >= 0)
    bias = rel_table[t5_bucket(jnp.maximum(rel, 0) * dilation)].transpose(2, 0, 1)

    s = jnp.einsum('brnqhd,brnkhd->brnhqk', qb, kw).astype(jnp.float32) * scale
    s = jnp.where(valid[:, None], s + bias.astype(jnp.float32), NEG_INF)
    m = jnp.max(s, axis=-1, keepdims=True)
    e = jnp.exp(s - m)
    denom = jnp.sum(e, axis=-1, keepdims=True)
    o = jnp.einsum('brnhqk,brnkhd->brnqhd', (e / denom).astype(v.dtype), vw)
    lse = (m + jnp.log(denom))[..., 0]

    o = o.reshape(B, dilation, Lp, H, Dh)[:, :, :L].transpose(0, 2, 1, 3, 4).reshape(B, S, H, Dh)
    lse = lse.transpose(0, 1, 2, 4, 3).reshape(B, dilation, Lp, H)[:, :, :L]
    lse = lse.transpose(0, 2, 1, 3).reshape(B, S, H)
    return o, lse

def token_mixer(h, w_in, b_f, w_o, rel_table):
    B, S, _ = h.shape
    u = h @ w_in
    splits = np.cumsum([D_FOX, D_FOX, D_FOX, N_HEADS_FOX, D_DIL, D_DIL]).tolist()
    qa, ka, va, f_logit, qb, kb, vb = jnp.split(u, splits, axis=-1)
    heads = lambda a, H: a.reshape(B, S, H, HEAD_DIM)

    log_f = jax.nn.log_sigmoid((f_logit + b_f).astype(jnp.float32))
    o_a = forgetting_attention(heads(qa, N_HEADS_FOX), heads(ka, N_HEADS_FOX),
                               heads(va, N_HEADS_FOX), log_f)

    qb, kb, vb = heads(qb, N_HEADS_DIL), heads(kb, N_HEADS_DIL), heads(vb, N_HEADS_DIL)
    outs, lses = [], []
    for window, dilation in DILATED_PATTERNS:
        o_i, lse_i = dilated_window_attention(qb, kb, vb, rel_table, window, dilation)
        outs.append(o_i)
        lses.append(lse_i)
    wts = jax.nn.softmax(jnp.stack(lses, axis=0), axis=0)
    o_b = jnp.sum(wts[..., None] * jnp.stack(outs, axis=0).astype(jnp.float32), axis=0).astype(h.dtype)

    cat = jnp.concatenate([o_a.reshape(B, S, D_FOX), o_b.reshape(B, S, D_DIL)], axis=-1)
    return cat @ w_o

def setup_inputs(seed: int = 0) -> dict:
    key = jax.random.key(seed)
    ks = jax.random.split(key, 24)
    nrm = lambda k, shape, s: jax.random.normal(k, shape, jnp.float32) * s
    gain = lambda k: 1.0 + 0.05 * jax.random.normal(k, (DEPTH, D_MODEL), jnp.float32)
    return {
        "x": nrm(ks[0], (BATCH, SEQ, D_MODEL), 1.0),
        "p": nrm(ks[1], (DEPTH, BATCH, SEQ, PLE_DIM), 1.0),
        "norm_ffn1": gain(ks[2]),
        "ffn1_w_gate": nrm(ks[3], (DEPTH, D_MODEL, D_FF), D_MODEL ** -0.5),
        "ffn1_w_up": nrm(ks[4], (DEPTH, D_MODEL, D_FF), D_MODEL ** -0.5),
        "ffn1_w_down": nrm(ks[5], (DEPTH, D_FF, D_MODEL), D_FF ** -0.5),
        "norm_mix": gain(ks[6]),
        "w_in": nrm(ks[7], (DEPTH, D_MODEL, D_IN_PROJ), D_MODEL ** -0.5),
        "b_f": 2.0 + nrm(ks[8], (DEPTH, N_HEADS_FOX), 0.1),
        "w_o": nrm(ks[9], (DEPTH, MIX_WIDTH, D_MODEL), MIX_WIDTH ** -0.5),
        "norm_ffn2": gain(ks[10]),
        "ffn2_w_gate": nrm(ks[11], (DEPTH, D_MODEL, D_FF), D_MODEL ** -0.5),
        "ffn2_w_up": nrm(ks[12], (DEPTH, D_MODEL, D_FF), D_MODEL ** -0.5),
        "ffn2_w_down": nrm(ks[13], (DEPTH, D_FF, D_MODEL), D_FF ** -0.5),
        "norm_ple": gain(ks[14]),
        "w_ple_gate": nrm(ks[15], (DEPTH, D_MODEL, D_MODEL), D_MODEL ** -0.5),
        "w_ple_proj": nrm(ks[16], (DEPTH, PLE_DIM, D_MODEL), PLE_DIM ** -0.5),
        "rel_table": nrm(ks[17], (N_REL_BUCKETS, N_HEADS_DIL), 0.5),
        "norm_final": 1.0 + 0.05 * jax.random.normal(ks[18], (D_MODEL,), jnp.float32),
    }

def reference(x, p, norm_ffn1, ffn1_w_gate, ffn1_w_up, ffn1_w_down, norm_mix, w_in, b_f, w_o,
              norm_ffn2, ffn2_w_gate, ffn2_w_up, ffn2_w_down, norm_ple, w_ple_gate, w_ple_proj,
              rel_table, norm_final):
    for i in range(DEPTH):
        x = x + 0.5 * swiglu(rmsnorm(x, norm_ffn1[i]), ffn1_w_gate[i], ffn1_w_up[i], ffn1_w_down[i])
        x = x + token_mixer(rmsnorm(x, norm_mix[i]), w_in[i], b_f[i], w_o[i], rel_table)
        x = x + 0.5 * swiglu(rmsnorm(x, norm_ffn2[i]), ffn2_w_gate[i], ffn2_w_up[i], ffn2_w_down[i])
        gate = jax.nn.sigmoid(rmsnorm(x, norm_ple[i]) @ w_ple_gate[i])
        x = x + gate * (p[i] @ w_ple_proj[i])
    return rmsnorm(x, norm_final)


_drawn_inputs = setup_inputs


def setup_inputs(seed=0):
    import zlib

    import numpy as np

    out = dict(_drawn_inputs(seed))
    spreads = {}
    factors = {'norm_ffn1': 2.674,
     'b_f': 24.752,
     'norm_ffn2': 3.314,
     'norm_ple': 52.91,
     'norm_mix': 6.443}
    for name, (base, spread) in spreads.items():
        noise = np.random.default_rng([zlib.crc32(name.encode()), seed]).standard_normal(out[name].shape)
        drawn = base * np.exp(spread * noise) if base else spread * noise
        out[name] = __import__('jax').numpy.asarray(drawn.astype(out[name].dtype))
    for name, factor in factors.items():
        out[name] = (out[name] * factor).astype(out[name].dtype)
    return out
```

```python
from contextlib import ExitStack

import numpy as np
import concourse.bass as bass
from concourse import mybir

P = 128
D = 2048
SEQ = 256
TB = SEQ // P
DFF = 5632
HD = 128
NF = ND = 8
NH = NF + ND
PLE = 256
DIN = 3 * NF * HD + NF + 3 * ND * HD
NW = 512
KT = D // P
KF = DFF // P
STRIPES = D // NW
FS = DFF // NW
HUK = 2
UK = 2 * HUK
NRAW = 4
NSPLIT = 4
GH = NW // HD
NEG = -1e30
EPS = 1e-6
NB = 32
QCOL = {0: 3 * NF * HD + NF, 1: 3 * NF * HD + NF + NW, 2: 0, 3: NW}
KSTEP = NF * HD


def shape_constants():
    i = np.arange(P)
    ident = np.eye(P, dtype=np.float32)
    flip = ident[::-1].copy()
    dist = P + i[:, None] - np.arange(2 * P)[None, :]
    causal = np.where(dist >= 0, 0.0, NEG).astype(np.float32)
    upto = (i[:, None] <= i[None, :]).astype(np.float32)
    after = np.concatenate([np.ones((P, P)), i[:, None] > i[None, :]], axis=1).astype(np.float32)
    one = np.ones((P, P), np.float32)
    square = np.ascontiguousarray(np.concatenate([ident, flip, causal, upto, one, after], axis=1))
    d = 255 - np.arange(3 * P)
    dd = np.maximum(d, 1).astype(np.float32)
    large = 16 + (np.log(dd / np.float32(16)) / np.float32(np.log(128.0)) * np.float32(16)).astype(np.int32)
    bucket = np.where(d < 16, d, np.minimum(large, NB - 1))
    bucket = np.where(d < 0, -1, bucket)
    onehot = (bucket[None, :] == np.arange(NB)[:, None]).astype(np.float32)
    count = (d <= 128).astype(int) + (d % 4 == 0) + (d % 16 == 0)
    count = np.where(d < 0, 0, count)
    lncount = np.where(count > 0, np.log(np.maximum(count, 1)), NEG).astype(np.float32)
    return square, onehot, np.ascontiguousarray(np.broadcast_to(lncount, (ND, 3 * P)))


SEGMENTS = [
    ("ffn1_first", 1, dict(h=16, u=8, j0=1, j1=1, f=10)),
    ("ffn1_loop", FS - 1, dict(h=16, u=8, j0=1, j1=1, f=2)),
    ("down1", 1, dict(h=88, u=44, j0=2, j1=2, f=8)),
    ("group0", 1, dict(h=24, u=12, j0=2, j1=1, f=10)),
    ("group1", 1, dict(h=24, u=12, j0=1, j1=2, f=8)),
    ("group2", 1, dict(h=24, u=12, j0=2, j1=1, f=8)),
    ("group3", 1, dict(h=24, u=12, j0=1, j1=2, f=8)),
    ("out", 1, dict(h=32, u=16, j0=2, j1=2, f=10)),
    ("ffn2_first", 1, dict(h=16, u=8, j0=1, j1=1, f=2)),
    ("ffn2_loop", FS - 1, dict(h=16, u=8, j0=1, j1=1, f=2)),
    ("down2", 1, dict(h=88, u=44, j0=2, j1=2, f=8)),
    ("ple", 1, dict(h=36, u=20, j0=4, j1=4, f=3)),
]
BASE = {}
_run = dict(h=0, u=0, j0=0, j1=0, f=0)
for _name, _times, _add in SEGMENTS:
    BASE[_name] = (dict(_run), _add)
    for _k in _run:
        _run[_k] += _times * _add[_k]
TOTAL = _run


class At:

    def __init__(self, name, it=None):
        self.base, self.rate = BASE[name]
        self.it = it

    def __call__(self, what, k=0):
        v = self.base[what] + k
        return v if self.it is None else v + self.it * self.rate[what]

    def slot(self, what, k, n):
        assert self.it is None or self.rate[what] % n == 0
        return (self.base[what] + k) % n

    def uses(self, u):
        v = 16 * ((self.base["u"] + u) // NRAW + 1)
        return v if self.it is None else v + self.it * (16 * self.rate["u"] // NRAW)

    def drained(self, par, n, tb):
        v = 2 * (self.base[f"j{par}"] + n) + tb + 1
        return v if self.it is None else v + self.it * (2 * self.rate[f"j{par}"])


def wait(eng, sem, value):
    if not isinstance(value, int) or value > 0:
        eng.wait_ge(sem, value)


def ple_units():
    out, u = [], 0
    for s in range(4):
        for i in range(8):
            out.append((u + i // 2, i % 2))
        out.append((u + 4, 0))
        u += 5
    return out


PLE_HUS = ple_units()


def hybrid_layer(nc, x, p, norm_ffn1, ffn1_w_gate, ffn1_w_up, ffn1_w_down, norm_mix, w_in, b_f, w_o,
                 norm_ffn2, ffn2_w_gate, ffn2_w_up, ffn2_w_down, norm_ple, w_ple_gate, w_ple_proj,
                 rel_table, norm_final, c_square, c_onehot, c_lncount, out):
    F = mybir.dt.float32
    R = mybir.dt.float32r
    ALU = mybir.AluOpType
    ACT = mybir.ActivationFunctionType
    AX = mybir.AxisListType
    ds = bass.ds
    QSCALE = float(HD) ** -0.5

    bias_rows = nc.dram_tensor("bias_rows", [ND, 3 * P], F, kind="Internal")

    at_byte = [(nc.sbuf_base + 31) // 32 * 32]

    def place(name, shape, dt):
        size = 4 * int(np.prod(shape[1:]))
        t = nc.alloc_sbuf_tensor_at(name, shape, dt, offset=at_byte[0])
        at_byte[0] += (size + 31) // 32 * 32
        return t

    x_sb = place("x_sb", [P, TB, D], F)
    xT_hi = place("xT_hi", [P, KT, SEQ], R)
    xT_lo = place("xT_lo", [P, KT, SEQ], R)
    raw = place("raw", [P, NRAW, UK, NW], F)
    w_hi = place("w_hi", [P, NSPLIT, HUK, NW], R)
    w_lo = place("w_lo", [P, NSPLIT, HUK, NW], R)
    sg = place("sg", [P, TB, NW], F)
    ident = place("ident", [P, P], F)
    gain_rows = place("gain_rows", [KT, P], F)
    later_gain_rows = place("later_gain_rows", [3 * KT, P], F)
    gains = place("gains", [P, 4 * KT], F)
    ssq = place("ssq", [P, TB, STRIPES], F)
    var = place("var", [P, 5, TB], F)
    sd = place("sd", [P, 5, TB], F)
    rstd = place("rstd", [P, 5, TB], F)
    newton = place("newton", [P, TB], F)
    qs = place("qs", [P, TB], F)

    shared = at_byte[0]

    hT = []
    for n in (1, 2):
        at_byte[0] = shared
        hT.append((place(f"hT{n}_hi", [P, KF, SEQ], R), place(f"hT{n}_lo", [P, KF, SEQ], R)))

    at_byte[0] = shared
    oT_hi = place("oT_hi", [P, NH, SEQ], R)
    oT_lo = place("oT_lo", [P, NH, SEQ], R)
    qT = place("qT", [P, GH, SEQ], F)
    kT = place("kT", [P, GH, SEQ], F)
    v_sb = place("v_sb", [P, TB, NW], F)
    square = place("square", [P, 8 * P], F)
    flip = square[:, P:2 * P]
    causal = square[:, 2 * P:4 * P]
    upto = square[:, 4 * P:5 * P]
    ones = square[:, 5 * P:6 * P]
    after = square[:, 6 * P:8 * P]
    bias = place("bias", [P, ND, SEQ], F)
    bias_shifted = place("bias_shifted", [P, ND, SEQ], F)
    table = place("table", [NB, ND], F)
    onehot = place("onehot", [NB, 3 * P], F)
    lncount = place("lncount", [ND, 3 * P], F)
    bias_row = place("bias_row", [ND, 3 * P], F)
    fw = place("fw", [P, KT, NF], F)
    zT = place("zT", [2 * NF, SEQ], F)
    z_parts = place("z_parts", [P, TB, 2, NF], F)
    bf = place("bf", [P, NF], F)
    fz = place("fz", [P, 6, TB, NF], F)
    fw_parts = nc.alloc_sbuf_tensor_at("fw_parts", [P, KT, P], R, offset=at_byte[0])
    decay = place("decay", [P, NF, 3, P], F)
    scores = place("scores", [P, 2, 3 * P], F)
    pT_sb = place("pT_sb", [P, 2, 3 * P], F)
    row_max = place("row_max", [P, 2, 2], F)
    neg_max = place("neg_max", [P, 2, 2], F)
    denom = place("denom", [P, 2, 2], F)
    rdenom = place("rdenom", [P, 2, 2], F)
    assert at_byte[0] <= nc.sbuf_usable_end, at_byte[0]

    at_byte[0] = shared
    p_sb = place("p_sb", [P, TB, PLE], F)
    pT_hi = place("pT_hi", [P, PLE // P, SEQ], R)
    pT_lo = place("pT_lo", [P, PLE // P, SEQ], R)
    gfin = place("gfin", [P, D], F)
    out_sb = place("out_sb", [P, TB, D], F)

    with ExitStack() as ctx:
        psum = lambda name: ctx.enter_context(nc.psum_tensor(name, [P, NW], F))
        sem = lambda name: ctx.enter_context(nc.semaphore(name))
        acc = [[psum(f"acc{par}{tb}") for tb in range(TB)] for par in range(2)]
        T = [psum("T0"), psum("T1")]
        X0, X1 = psum("X0"), psum("X1")

        x_in = [sem(f"x_in{s}") for s in range(STRIPES)]
        consts_in = sem("consts_in")
        gains_in = sem("gains_in")
        raw_in = [sem(f"raw_in{n}") for n in range(NRAW)]
        hi_done = sem("hi_done")
        lo_done = sem("lo_done")
        mm_done = sem("mm_done")
        drained = [sem(f"drained{par}") for par in range(2)]
        t_filled = sem("t_filled")
        t_act = sem("t_act")
        t_dve = sem("t_dve")
        sq_done = sem("sq_done")
        var_done = sem("var_done")
        sd_done = sem("sd_done")
        rstd_done = sem("rstd_done")
        dve_step = sem("dve_step")
        mix_in = sem("mix_in")
        row_filled = sem("row_filled")
        row_done = sem("row_done")
        row_out = sem("row_out")
        shifted_in = sem("shifted_in")
        fw_split = sem("fw_split")
        fw_zero = sem("fw_zero")
        f_filled = sem("f_filled")
        zT_done = sem("zT_done")
        f_arg = sem("f_arg")
        f_act = sem("f_act")
        logf_done = sem("logf_done")
        decay_done = sem("decay_done")
        scored = sem("scored")
        masked = sem("masked")
        e_done = sem("e_done")
        p_done = sem("p_done")
        pT_filled = sem("pT_filled")
        pT_done = sem("pT_done")
        ple_in = sem("ple_in")
        x_last = sem("x_last")
        gained = sem("gained")
        out_ready = [sem(f"out_ready{s}") for s in range(STRIPES)]
        stored = sem("stored")
        block = ctx.enter_context(nc.Block())

        def tiles(w, k0, c0, nk=UK, width=NW):
            rows = w[k0 * P:(k0 + nk) * P, c0:c0 + width] if isinstance(c0, int) else \
                w[k0 * P:(k0 + nk) * P, ds(c0, width)]
            return rows.rearrange("(t p) c -> p t c", p=P)

        gate_up = [(ffn1_w_gate[0], ffn1_w_up[0]), (ffn2_w_gate[0], ffn2_w_up[0])]
        down = [ffn1_w_down[0], ffn2_w_down[0]]
        OUT_UNITS = [(0, u) for u in (2, 3, 0)] + [(1, u) for u in (2, 3, 0)] + [(0, 1), (1, 1)] + \
            [(s, u) for s in (2, 3) for u in range(4)]

        xT = (xT_hi, xT_lo)

        def job_hus(par, lhs, n):
            return [(par, lhs, HUK * i, i == 0, i == n - 1) for i in range(n)]

        FFN_HUS = job_hus(0, xT, 8) + job_hus(1, xT, 8)
        DOWN_HUS = [sum((job_hus(s % 2, hT[n], 22) for s in range(STRIPES)), []) for n in range(2)]
        GROUP_HUS = [sum((job_hus((3 * g + j) % 2, xT, 8) for j in range(3)), []) for g in range(4)]
        oT = (oT_hi, oT_lo)
        OUT_HUS = []
        for n, (s, u) in enumerate(OUT_UNITS):
            for half in range(2):
                opens = (n in (0, 3) or (n >= 8 and u == 0)) and half == 0
                closes = (n in (6, 7) or (n >= 8 and u == 3)) and half == 1
                OUT_HUS.append((s % 2, oT, UK * u + HUK * half, opens, closes))
        PLE_STEPS = sum((job_hus(0, xT, 8) + job_hus(1, (pT_hi, pT_lo), 1) for s in range(STRIPES)), [])
        OUT_END = [14, 16, 24, 32]

        @block.sync
        def _(sp):
            def load(at, u, src, last_hu_before, dst=None):
                wait(sp, lo_done, last_hu_before)
                slot = at.slot("u", u, NRAW)
                sp.dma_start(raw[:, slot] if dst is None else raw[:, slot, 0:dst], src)\
                    .then_inc(raw_in[slot], 16)

            def free(at, u):
                return at("h", 2 * (u - NRAW) + 2)

            def ffn_units(at, n, col):
                for u in range(8):
                    load(at, u, tiles(gate_up[n][u // 4], UK * (u % 4), col), free(at, u))

            gain_of = lambda g: g[0].rearrange("(t p) -> t p", p=P)
            sp.dma_start(ident[:, :], c_square[:, 0:P]).then_inc(consts_in, 16)
            sp.dma_start(gain_rows[:, :], gain_of(norm_ffn1)).then_inc(consts_in, 16)
            xv = x[0].rearrange("(b p) d -> p b d", p=P)
            at = At("ffn1_first")
            for s in range(STRIPES):
                sp.dma_start(x_sb[:, :, s * NW:(s + 1) * NW], xv[:, :, s * NW:(s + 1) * NW])\
                    .then_inc(x_in[s], 16)
                load(at, s, tiles(gate_up[0][0], UK * s, 0), 0)
            for n, g in enumerate((norm_mix, norm_ffn2, norm_ple)):
                sp.dma_start(later_gain_rows[n * KT:(n + 1) * KT, :], gain_of(g)).then_inc(gains_in, 16)
            for u in range(4, 8):
                load(at, u, tiles(gate_up[0][1], UK * (u - 4), 0), free(at, u))
            for n in range(2):
                if n == 1:
                    ffn_units(At("ffn2_first"), 1, 0)
                with sp.Fori(0, FS - 1) as it:
                    ffn_units(At(f"ffn{n + 1}_loop", it), n, it * NW + NW)
                at = At(f"down{n + 1}")
                for s in range(STRIPES):
                    for k in range(FS):
                        u = s * FS + k
                        load(at, u, tiles(down[n], UK * k, s * NW), free(at, u))
                if n == 0:
                    for g in range(4):
                        at = At(f"group{g}")
                        for u in range(12):
                            load(at, u, tiles(w_in[0], UK * (u % 4), QCOL[g] + KSTEP * (u // 4)), free(at, u))
                    at = At("out")
                    for u, (s, k) in enumerate(OUT_UNITS):
                        load(at, u, tiles(w_o[0], UK * k, s * NW), free(at, u))
            at = At("ple")
            last = {u: i for i, (u, _) in enumerate(PLE_HUS)}
            for u in range(20):
                before = at("h", last[u - NRAW] + 1) if u >= NRAW else free(at, u)
                s, k = divmod(u, 5)
                if k < 4:
                    load(at, u, tiles(w_ple_gate[0], UK * k, s * NW), before)
                else:
                    load(at, u, tiles(w_ple_proj[0], 0, s * NW, HUK), before, HUK)
            ov = out[0].rearrange("(b p) d -> p b d", p=P)
            for s in (0, 3, 1, 2):
                sp.wait_ge(out_ready[s], TB)
                sp.dma_start(ov[:, :, s * NW:(s + 1) * NW], out_sb[:, :, s * NW:(s + 1) * NW]).then_inc(stored, 16)
            sp.wait_ge(stored, 16 * STRIPES)

        @block.gpsimd
        def _(pool):
            pool.wait_ge(mm_done, At("group0")("h"))
            for dst, src in (
                (table[:, :], rel_table), (onehot[:, :], c_onehot), (lncount[:, :], c_lncount),
                (square[:, :], c_square), (bf[:, :], b_f[0].partition_broadcast(P)),
                (fw[:, :, :], w_in[0][:, 3 * NF * HD:3 * NF * HD + NF].rearrange("(t p) c -> p t c", p=P)),
            ):
                pool.dma_start(dst, src).then_inc(mix_in, 16)
            nc.gpsimd.memset(fw_parts[:, :, 2 * NF:P].bitcast(F), 0.0).then_inc(fw_zero, 1)
            pool.wait_ge(row_done, 1)
            pool.dma_start(bias_rows.ap(), bias_row[:, :]).then_inc(row_out, 16)
            pool.wait_ge(row_out, 16)
            shifted = bass.AP(bias_rows, 0, [[1, P], [3 * P, ND], [1, SEQ]])
            pool.dma_start(bias_shifted[:, :, :], shifted).then_inc(shifted_in, 16)
            pool.wait_ge(mix_in, 16 * 6)
            pool.wait_ge(logf_done, 1)
            for h in range(NF):
                nc.gpsimd.tensor_scalar(decay[:, h, 0, :], ones, fz[:, 0, 0, h:h + 1], None, ALU.mult)
                nc.gpsimd.tensor_scalar(decay[:, h, 1, :], upto, fz[:, 0, 1, h:h + 1], None, ALU.mult)
                nc.gpsimd.tensor_scalar(decay[:, h, 2, :], upto, fz[:, 0, 0, h:h + 1], None, ALU.mult)\
                    .then_inc(decay_done, 1)
            pool.wait_ge(mm_done, At("ple")("h"))
            pool.dma_start(p_sb[:, :, :], p[0, 0].rearrange("(b p) d -> p b d", p=P)).then_inc(ple_in, 16)
            pool.dma_start(gfin[:, :], norm_final.partition_broadcast(P)).then_inc(ple_in, 16)
            pool.wait_ge(ple_in, 32)
            for s in range(STRIPES - 1):
                pool.wait_ge(x_last, TB * (s + 1))
                cols = slice(s * NW, (s + 1) * NW)
                for tb in range(TB):
                    last = nc.gpsimd.tensor_tensor(out_sb[:, tb, cols], x_sb[:, tb, cols], gfin[:, cols], ALU.mult)
                last.then_inc(gained, 1)

        @block.tensor
        def _(pe):
            fill = [0]

            def products(at, i, hu):
                par, (hi, lo), kt, opens, closes = hu
                if opens:
                    wait(pe, drained[par], pe_jobs[par](at))
                wait(pe, lo_done, at("h", i + 1))
                slot = at.slot("h", i, NSPLIT)
                for k in range(HUK):
                    for tb in range(TB):
                        tok = slice(tb * P, (tb + 1) * P)
                        for n, (a, w) in enumerate(((hi, w_hi), (hi, w_lo), (lo, w_hi))):
                            last = nc.tensor.matmul(
                                acc[par][tb][:, :], a[:, kt + k, tok], w[:, slot, k, :],
                                start=opens and k == 0 and n == 0, stop=closes and k == HUK - 1 and n == 2)
                last.then_inc(mm_done, 1)

            opened = [0, 0]

            def jobs_before(par):
                def value(at):
                    n = opened[par]
                    opened[par] += 1
                    return at.drained(par, n, TB - 1) - 2
                return value

            pe_jobs = [jobs_before(0), jobs_before(1)]

            def open_fill():
                f = fill[0]
                fill[0] += 1
                wait(pe, t_act, at("f", f - 1))
                wait(pe, t_dve, at("f", f - 1))
                return T[at.slot("f", f, 2)]

            def transposes(src, blocks, bank):
                for k, tb in blocks:
                    last = nc.tensor.transpose(bank[:, (k % 2) * SEQ + tb * P:(k % 2) * SEQ + (tb + 1) * P],
                                               src(k, tb), ident[:, :])
                last.then_inc(t_filled, 1)

            def x_stripe(s):
                for half in range(2):
                    bank = open_fill()
                    transposes(lambda k, tb: x_sb[:, tb, (4 * s + k) * P:(4 * s + k + 1) * P],
                               [(2 * half + k, tb) for k in range(2) for tb in range(TB)], bank)

            def sg_stripe():
                for half in range(2):
                    bank = open_fill()
                    transposes(lambda k, tb: sg[:, tb, k * P:(k + 1) * P],
                               [(2 * half + k, tb) for k in range(2) for tb in range(TB)], bank)

            def after_drain(par, n, what):
                def go():
                    pe.wait_ge(drained[par], at.drained(par, n, TB - 1))
                    what()
                return go

            def run(hus, hooks):
                for i, hu in enumerate(hus):
                    if i in hooks:
                        hooks[i]()
                    if i in ready:
                        wait(pe, t_dve, at("f", ready[i]))
                        wait(pe, t_act, at("f", ready[i]))
                    products(at, i, hu)

            def segment(name, it=None):
                fill[0] = 0
                opened[0] = opened[1] = 0
                return At(name, it)

            ready = {}
            at = segment("ffn1_first")
            pe.wait_ge(consts_in, 16 * 2)
            nc.tensor.transpose(open_fill()[:, 0:KT], gain_rows[:, :], ident[0:KT, 0:KT]).then_inc(t_filled, 1)

            def later_gains():
                pe.wait_ge(gains_in, 16 * 3)
                nc.tensor.transpose(open_fill()[:, 0:3 * KT], later_gain_rows[:, :], ident[0:3 * KT, 0:3 * KT])\
                    .then_inc(t_filled, 1)

            def first_stripe(s):
                def go():
                    pe.wait_ge(x_in[s], 16)
                    x_stripe(s)
                return go

            first_stripe(0)()
            ready = {0: 3, 2: 5, 4: 7, 6: 9}
            run(FFN_HUS, {**{2 * (s - 1): first_stripe(s) for s in range(1, STRIPES)}, 9: later_gains})

            def ffn_rest(n):
                nonlocal at, ready
                ready = {}
                with pe.Fori(0, FS - 1) as it:
                    at = segment(f"ffn{n + 1}_loop", it)
                    run(FFN_HUS, {2: after_drain(1, -1, sg_stripe)})
                at = segment(f"down{n + 1}")
                ready = {0: 0, 20: 2}
                hooks = {2: after_drain(1, -1, sg_stripe)}
                for s in range(STRIPES - 1):
                    hooks[22 * (s + 1) + 1] = after_drain(s % 2, s // 2, lambda s=s: x_stripe(s))
                run(DOWN_HUS[n], hooks)

            def score(a):
                i = a % GH
                fox = a >= ND
                if i == 0:
                    pe.wait_ge(t_act, group_qk[0])
                    pe.wait_ge(t_dve, group_qk[0])
                if a == 0:
                    pe.wait_ge(sq_done, 8 * 2)
                if fox:
                    pe.wait_ge(decay_done, a - ND + 1)
                wait(pe, masked, a)
                S1, S0 = X0[:, 0:SEQ], X0[:, SEQ:SEQ + P]
                nc.tensor.matmul(S1, qT[:, i, P:2 * P], kT[:, i, :], start=True, stop=not fox)
                if fox:
                    h = a - ND
                    nc.tensor.matmul(X0[:, 0:P], decay[:, h, 0, :], after[:, P:2 * P], start=False, stop=False)
                    nc.tensor.matmul(S1, decay[:, h, 1, :], after, start=False, stop=True)
                last = nc.tensor.matmul(S0, qT[:, i, 0:P], kT[:, i, 0:P], start=True, stop=not fox)
                if fox:
                    last = nc.tensor.matmul(S0, decay[:, h, 2, :], after[:, P:2 * P], start=False, stop=True)
                last.then_inc(scored, 1)

            def turn(a):
                pe.wait_ge(p_done, a + 1)
                wait(pe, pT_done, a)
                S = scores[:, a % 2]
                nc.tensor.transpose(X1[:, 0:P], S[:, SEQ:SEQ + P], ident[:, :])
                nc.tensor.transpose(X1[:, P:2 * P], S[:, 0:P], ident[:, :])
                nc.tensor.transpose(X1[:, 2 * P:3 * P], S[:, P:2 * P], ident[:, :]).then_inc(pT_filled, 1)

            def weigh(a):
                i = a % GH
                if i == 0:
                    pe.wait_ge(drained[group_v[0]], group_v[1])
                pe.wait_ge(pT_done, a + 1)
                bank = open_fill()
                nc.tensor.matmul(bank[:, 0:SEQ], v_sb[:, 0, i * HD:(i + 1) * HD], pT_sb[:, a % 2, 0:SEQ],
                                 start=True, stop=False)
                nc.tensor.matmul(bank[:, P:SEQ], v_sb[:, 1, i * HD:(i + 1) * HD], pT_sb[:, a % 2, SEQ:3 * P],
                                 start=False, stop=True).then_inc(t_filled, 1)

            group_qk = [0]
            group_v = [0, 0]

            def t5_rows():
                pe.wait_ge(mix_in, 16 * 6)
                nc.tensor.matmul(X1[0:ND, 0:3 * P], table[:, :], onehot[:, :], start=True, stop=True)\
                    .then_inc(row_filled, 1)

            def forget_logits():
                pe.wait_ge(fw_zero, 1)
                pe.wait_ge(fw_split, 2)
                pe.wait_ge(row_done, 1)
                for k in range(KT):
                    for n, a in enumerate(xT):
                        last = nc.tensor.matmul(X1[:, 0:SEQ], fw_parts[:, k, :], a[:, k, :],
                                                start=k == 0 and n == 0, stop=k == KT - 1 and n == 1)
                last.then_inc(f_filled, 1)

            def forget_tokens():
                pe.wait_ge(zT_done, 1)
                for tb in range(TB):
                    last = nc.tensor.transpose(X1[:, tb * 2 * NF:(tb + 1) * 2 * NF], zT[:, tb * P:(tb + 1) * P],
                                               ident[0:2 * NF, 0:2 * NF])
                last.then_inc(f_filled, 1)

            def flip_bias(pair):
                pe.wait_ge(shifted_in, 16)
                for n in (pair, pair + 1):
                    bank = open_fill()
                    nc.tensor.matmul(bank[:, :], flip, bias_shifted[:, 2 * n:2 * n + 2, :], start=True, stop=True)\
                        .then_inc(t_filled, 1)

            ffn_rest(0)
            for g in range(4):
                at = segment(f"group{g}")
                qpar, kpar = 3 * g % 2, (3 * g + 1) % 2
                hooks = {14: after_drain(qpar, 0, sg_stripe), 19: after_drain(kpar, 0, sg_stripe)}
                ready = {}
                if g == 0:
                    ready = {0: 0, 6: 2}
                    hooks[1] = after_drain(1, -1, lambda: x_stripe(3))
                    hooks[8] = t5_rows
                    hooks[12] = forget_logits
                    hooks[13] = forget_tokens
                    hooks[16] = lambda: flip_bias(0)
                    hooks[20] = lambda: flip_bias(2)
                else:
                    for i in range(GH):
                        a = GH * (g - 1) + i
                        hooks[4 * i] = lambda a=a: score(a)
                        hooks[4 * i + 3] = lambda a=a: turn(a)
                        hooks[4 * i + 5] = lambda a=a: weigh(a)
                run(GROUP_HUS[g], hooks)
                group_qk[0] = at("f", fill[0])
                group_v = [qpar, at.drained(qpar, 1, TB - 1)]
            at = segment("out")
            ready = {0: 0, 12: 4}
            hooks = {}
            for i in range(GH):
                a = 3 * GH + i
                hooks[2 * i] = lambda a=a, i=i: (score(a), i > 0 and turn(a - 1), i > 1 and weigh(a - 2))
            hooks[8] = lambda: (turn(15), weigh(14))
            hooks[10] = lambda: weigh(15)
            for s in range(STRIPES - 1):
                hooks[OUT_END[s] + 2 - (s >= 2)] = after_drain(s % 2, s // 2, lambda s=s: x_stripe(s))
            run(OUT_HUS, hooks)

            at = segment("ffn2_first")
            ready = {0: 0, 6: 2}
            run(FFN_HUS, {1: after_drain(1, -1, lambda: x_stripe(3))})
            ffn_rest(1)
            at = segment("ple")
            ready = {0: 0, 6: 2, 8: 3}

            def embedding():
                pe.wait_ge(ple_in, 32)
                bank = open_fill()
                transposes(lambda k, tb: p_sb[:, tb, k * P:(k + 1) * P],
                           [(k, tb) for k in range(2) for tb in range(TB)], bank)

            run(PLE_STEPS, {1: after_drain(1, -1, lambda: x_stripe(3)), 5: embedding})

        @block.scalar
        def _(act):
            fill = [0]
            squared = [0]

            def split(at, i, unit=None):
                u, half = unit or (i // 2, i % 2)
                if half == 0:
                    act.wait_ge(raw_in[at.slot("u", u, NRAW)], at.uses(u))
                wait(act, mm_done, at("h", i - NSPLIT + 1))
                nc.scalar.activation(w_hi[:, at.slot("h", i, NSPLIT)],
                                     raw[:, at.slot("u", u, NRAW), HUK * half:HUK * half + HUK, :], ACT.Copy)\
                    .then_inc(hi_done, 1)

            def next_fill():
                f = fill[0]
                fill[0] += 1
                act.wait_ge(t_filled, at("f", f + 1))
                return T[at.slot("f", f, 2)]

            def x_stripe_hi(norm, s):
                for half in range(2):
                    bank = next_fill()
                    for k in range(2):
                        kt = 4 * s + 2 * half + k
                        last = nc.scalar.activation(xT_hi[:, kt, :], bank[:, k * SEQ:(k + 1) * SEQ], ACT.Copy,
                                                    scale=gains[:, norm * KT + kt:norm * KT + kt + 1])
                    last.then_inc(t_act, 1)

            def squares(s, before=lambda tb: None):
                for tb in range(TB):
                    before(tb)
                    wait(act, sq_done, squared[0])
                    squared[0] += 1
                    nc.scalar.activation(X0[:, :], x_sb[:, tb, s * NW:(s + 1) * NW], ACT.Square,
                                         accum_out=ssq[:, tb, s:s + 1]).then_inc(sq_done, 1)

            def roots(norm):
                act.wait_ge(var_done, norm + 1)
                nc.scalar.activation(sd[:, norm, :], var[:, norm, :], ACT.Sqrt).then_inc(sd_done, 1)

            def h_hi(n, kt):
                for half in range(2):
                    bank = next_fill()
                    at_kt = ds(kt + 2 * half, 2) if not isinstance(kt, int) else slice(kt + 2 * half, kt + 2 * half + 2)
                    nc.scalar.activation(hT[n][0][:, at_kt, :], bank[:, :].rearrange("p (k t) -> p k t", k=2),
                                         ACT.Copy).then_inc(t_act, 1)

            def gate(par, n, end, norm, func):
                act.wait_ge(mm_done, at("h", end))
                act.wait_ge(rstd_done, norm + 1)
                for tb in range(TB):
                    nc.scalar.activation(sg[:, tb, :], acc[par][tb][:, :], func, scale=rstd[:, norm, tb:tb + 1])\
                        .then_inc(drained[par], 1)

            def silu(norm):
                gate(0, 0, 8, norm, ACT.Silu)

            def run(n, hooks, units=None):
                for i in range(n):
                    for go in hooks.get(i, ()):
                        go()
                    split(at, i, units and units[i])

            def segment(name, it=None):
                fill[0] = 0
                return At(name, it)

            def stage_entry(norm):
                def wait_x():
                    act.wait_ge(drained[1], at.drained(1, -1, TB - 1))
                    squares(3)
                return {4: [lambda: x_stripe_hi(norm, 3)], 5: [wait_x], 7: [lambda: roots(norm)]}

            def x_hooks(norm, s, end):
                def wait_x():
                    act.wait_ge(drained[s % 2], at.drained(s % 2, s // 2, TB - 1))
                    squares(s)
                return {end + 4: [lambda: x_stripe_hi(norm, s)], end + 5: [wait_x]}

            def merge(*many):
                all_ = {}
                for hooks in many:
                    for i, go in hooks.items():
                        all_.setdefault(i, []).extend(go)
                return all_

            at = segment("ffn1_first")
            nc.scalar.activation(gains[:, 0:KT], next_fill()[:, 0:KT], ACT.Copy).then_inc(t_act, 1)
            act.wait_ge(t_act, 1)

            def later_gains():
                nc.scalar.activation(gains[:, KT:4 * KT], next_fill()[:, 0:3 * KT], ACT.Copy).then_inc(t_act, 1)

            def first(s):
                def go():
                    act.wait_ge(x_in[s], 16)
                    squares(s)
                return go

            run(16, merge({2 * s: [lambda s=s: x_stripe_hi(0, s)] for s in range(STRIPES)},
                          {i: [first(s)] for s, i in enumerate((5, 7, 8, 9))},
                          {10: [lambda: roots(0)], 12: [lambda: silu(0)], 13: [later_gains]}))

            def ffn_rest(n):
                nonlocal at
                norm = (0, 2)[n]
                with act.Fori(0, FS - 1) as it:
                    at = segment(f"ffn{n + 1}_loop", it)
                    run(16, {5: [lambda: h_hi(n, it * 4)], 11: [lambda: silu(norm)]})
                at = segment(f"down{n + 1}")
                run(88, merge({5: [lambda: h_hi(n, UK * (FS - 1))]},
                              *(x_hooks(norm + 1, s, 22 * (s + 1)) for s in range(STRIPES - 1))))

            def half_copy(dst):
                bank = next_fill()
                nc.scalar.activation(dst, bank[:, 0:SEQ], ACT.Copy).then_inc(t_act, 1)

            def split_fw():
                act.wait_ge(mix_in, 16 * 6)
                nc.scalar.activation(fw_parts[:, :, 0:NF], fw[:, :, :], ACT.Copy).then_inc(fw_split, 1)

            def forget_exp():
                act.wait_ge(f_arg, 1)
                nc.scalar.activation(fz[:, 2], fz[:, 1], ACT.Exp).then_inc(f_act, 1)

            def forget_ln():
                act.wait_ge(f_arg, 2)
                nc.scalar.activation(fz[:, 4], fz[:, 3], ACT.Ln).then_inc(f_act, 1)

            def token_major(par, n, end, dst, scale):
                act.wait_ge(mm_done, at("h", end))
                for tb in range(TB):
                    nc.scalar.activation(dst[:, tb, :], acc[par][tb][:, :], ACT.Copy, scale=scale[:, tb:tb + 1])\
                        .then_inc(drained[par], 1)

            def exps(a):
                act.wait_ge(masked, a + 1)
                S = scores[:, a % 2]
                nc.scalar.activation(S[:, 0:SEQ], S[:, 0:SEQ], ACT.Exp, bias=neg_max[:, a % 2, 0:1],
                                     accum_out=denom[:, a % 2, 0:1])
                nc.scalar.activation(S[:, SEQ:3 * P], S[:, SEQ:3 * P], ACT.Exp, bias=neg_max[:, a % 2, 1:2],
                                     accum_out=denom[:, a % 2, 1:2]).then_inc(e_done, 1)

            def p_copy(a):
                act.wait_ge(pT_filled, a + 1)
                nc.scalar.activation(pT_sb[:, a % 2, :], X1[:, 0:3 * P], ACT.Copy).then_inc(pT_done, 1)

            def head_hi(a):
                bank = next_fill()
                head = (a + NF) % NH
                nc.scalar.activation(oT_hi[:, head, :], bank[:, 0:SEQ], ACT.Copy).then_inc(t_act, 1)

            ffn_rest(0)
            rs = rstd[:, 1, :]
            for g in range(4):
                at = segment(f"group{g}")
                qpar, kpar = 3 * g % 2, (3 * g + 1) % 2

                def drain_q(par=qpar):
                    act.wait_ge(rstd_done, 2)
                    token_major(par, 0, 8, sg, qs)

                def drain_k(par=kpar, g=g):
                    act.wait_ge(t_filled, at("f", 4 if g == 0 else 5))
                    token_major(par, 0, 16, sg, rs)

                def copies(dst):
                    return lambda: [half_copy(dst[:, n, :]) for n in (0, 2)]

                def drain_v(par=1 - qpar):
                    token_major(par, 0, 0, v_sb, rs)

                hooks = merge({11: [drain_q], 17: [copies(qT)], 19: [drain_k], 22: [copies(kT)]})
                if g == 0:
                    hooks = merge(stage_entry(1), {11: [split_fw], 16: [forget_exp, forget_ln],
                                                   19: [lambda: [half_copy(bias[:, n, :]) for n in (0, 2)]],
                                                   23: [lambda: [half_copy(bias[:, n, :]) for n in (4, 6)]]},
                                  hooks)
                else:
                    steps = {3: [drain_v]}
                    for i in range(GH):
                        a = GH * (g - 1) + i
                        steps.setdefault(4 * i + 3, []).append(lambda a=a: exps(a))
                        steps.setdefault(4 * i + 6, []).append(lambda a=a: p_copy(a))
                        steps.setdefault(4 * i + 8, []).append(lambda a=a: head_hi(a))
                    hooks = merge(steps, hooks)
                run(24, hooks)
            at = segment("out")

            def drain_v_last():
                token_major(1, 0, 0, v_sb, rs)

            steps = {2: [drain_v_last]}
            for i in range(GH):
                a = 3 * GH + i
                steps.setdefault(2 * i + 2, []).append(lambda a=a: exps(a))
                steps.setdefault(2 * i + 4, []).append(lambda a=a: p_copy(a))
                steps.setdefault(2 * i + 6, []).append(lambda a=a: head_hi(a))
            run(32, merge(steps, *(x_hooks(2, s, OUT_END[s] + (s < 2)) for s in range(STRIPES - 1))))
            at = segment("ffn2_first")
            run(16, merge(stage_entry(2), {11: [lambda: silu(2)]}))
            ffn_rest(1)
            at = segment("ple")

            def embedding_hi():
                bank = next_fill()
                nc.scalar.activation(pT_hi[:, :, :], bank[:, :].rearrange("p (k t) -> p k t", k=2), ACT.Copy).then_inc(t_act, 1)

            def ple_gate(s):
                def go():
                    wait(act, x_last, TB * s)
                    gate(0, s, 9 * s + 8, 3, ACT.Sigmoid)
                return go

            def ple_squares(s):
                squares(s, lambda tb: act.wait_ge(x_last, TB * s + tb + 1))

            hooks = merge(stage_entry(3), {7: [embedding_hi]},
                          *({9 * s + 11: [ple_gate(s)], 9 * s + 14: [lambda s=s: ple_squares(s)]}
                            for s in range(STRIPES - 1)))
            run(36, hooks, PLE_HUS)
            ple_gate(3)()
            nc.scalar.activation(sd[:, 4, :], var[:, 3, :], ACT.Sqrt)
            ple_squares(3)
            roots(4)
            act.wait_ge(gained, STRIPES - 1)
            act.wait_ge(rstd_done, 5)
            for s in (1, 2):
                for tb in range(TB):
                    cols = slice(s * NW, (s + 1) * NW)
                    nc.scalar.activation(out_sb[:, tb, cols], out_sb[:, tb, cols], ACT.Copy,
                                         scale=rstd[:, 4, tb:tb + 1]).then_inc(out_ready[s], 1)

        @block.vector
        def _(dve):
            fill = [0]
            steps_done = [0]

            def split(at, i, unit=None):
                u, half = unit or (i // 2, i % 2)
                dve.wait_ge(hi_done, at("h", i + 1))
                slot = at.slot("h", i, NSPLIT)
                nc.vector.tensor_tensor(w_lo[:, slot], raw[:, at.slot("u", u, NRAW), HUK * half:HUK * half + HUK, :],
                                        w_hi[:, slot].bitcast(F), ALU.subtract).then_inc(lo_done, 1)

            def step(ins):
                steps_done[0] += 1
                ins.then_inc(dve_step, 1)
                dve.wait_ge(dve_step, steps_done[0])

            def next_fill():
                f = fill[0]
                fill[0] += 1
                dve.wait_ge(t_act, at("f", f + 1))
                return T[at.slot("f", f, 2)]

            def seen_fill():
                next_fill()
                dve.sem_inc(t_dve, 1)

            def x_stripe_lo(norm, s):
                for half in range(2):
                    bank = next_fill()
                    for k in range(2):
                        kt = 4 * s + 2 * half + k
                        last = nc.vector.scalar_tensor_tensor(
                            out=xT_lo[:, kt, :], in0=bank[:, k * SEQ:(k + 1) * SEQ],
                            scalar=gains[:, norm * KT + kt:norm * KT + kt + 1], in1=xT_hi[:, kt, :].bitcast(F),
                            op0=ALU.mult, op1=ALU.subtract)
                    last.then_inc(t_dve, 1)

            def h_lo(n, kt):
                for half in range(2):
                    bank = next_fill()
                    at_kt = ds(kt + 2 * half, 2) if not isinstance(kt, int) else slice(kt + 2 * half, kt + 2 * half + 2)
                    nc.vector.tensor_tensor(hT[n][1][:, at_kt, :], bank[:, :].rearrange("p (k t) -> p k t", k=2),
                                            hT[n][0][:, at_kt, :].bitcast(F), ALU.subtract).then_inc(t_dve, 1)

            def product(norm):
                def go():
                    dve.wait_ge(mm_done, at("h"))
                    dve.wait_ge(drained[0], at.drained(0, -1, TB - 1))
                    for tb in range(TB):
                        nc.vector.scalar_tensor_tensor(out=sg[:, tb, :], in0=acc[1][tb][:, :],
                                                       scalar=rstd[:, norm, tb:tb + 1], in1=sg[:, tb, :],
                                                       op0=ALU.mult, op1=ALU.mult).then_inc(drained[1], 1)
                return go

            def add_x(par, s, end, scale):
                def go():
                    dve.wait_ge(mm_done, at("h", end))
                    cols = slice(s * NW, (s + 1) * NW)
                    for tb in range(TB):
                        nc.vector.scalar_tensor_tensor(out=x_sb[:, tb, cols], in0=acc[par][tb][:, :], scalar=scale,
                                                       in1=x_sb[:, tb, cols], op0=ALU.mult, op1=ALU.add)\
                            .then_inc(drained[par], 1)
                return go

            def mean_square(norm):
                dve.wait_ge(sq_done, 2 * STRIPES * (norm + 1))
                step(nc.vector.reduce_sum(newton[:, :], ssq[:, :, :], AX.X))
                nc.vector.tensor_scalar(var[:, norm, :], newton[:, :], 1.0 / D, EPS, ALU.mult, ALU.add)\
                    .then_inc(var_done, 1)

            def inverse_root(norm):
                dve.wait_ge(sd_done, norm + 1)
                r = rstd[:, norm, :]
                step(nc.vector.reciprocal(r, sd[:, norm, :]))
                step(nc.vector.tensor_tensor(newton[:, :], var[:, norm, :], r, ALU.mult))
                step(nc.vector.tensor_tensor(newton[:, :], newton[:, :], r, ALU.mult))
                step(nc.vector.tensor_scalar(newton[:, :], newton[:, :], -0.5, 1.5, ALU.mult, ALU.add))
                if norm == 1:
                    step(nc.vector.tensor_tensor(r, r, newton[:, :], ALU.mult))
                    nc.vector.tensor_scalar(qs[:, :], r, QSCALE, None, ALU.mult).then_inc(rstd_done, 1)
                else:
                    nc.vector.tensor_tensor(r, r, newton[:, :], ALU.mult).then_inc(rstd_done, 1)
                dve.wait_ge(rstd_done, norm + 1)

            def run(n, hooks, units=None):
                for i in range(n):
                    for go in hooks.get(i, ()):
                        go()
                    split(at, i, units and units[i])

            def segment(name, it=None):
                fill[0] = 0
                return At(name, it)

            def merge(*many):
                all_ = {}
                for hooks in many:
                    for i, go in hooks.items():
                        all_.setdefault(i, []).extend(go)
                return all_

            def stage_entry(norm, scale):
                return {3: [add_x(1, 3, 0, scale)], 4: [lambda: x_stripe_lo(norm, 3)],
                        7: [lambda: mean_square(norm)], 8: [lambda: inverse_root(norm)]}

            def x_hooks(norm, s, end, scale, later=0):
                return {end + 3 + later: [add_x(s % 2, s, end, scale)],
                        end + 4 + later: [lambda: x_stripe_lo(norm, s)]}

            at = segment("ffn1_first")
            seen_fill()
            run(16, merge({2 * s: [lambda s=s: x_stripe_lo(0, s)] for s in range(STRIPES)},
                          {10: [lambda: mean_square(0)], 11: [lambda: inverse_root(0)], 13: [seen_fill]}))

            def ffn_rest(n):
                nonlocal at
                norm = (0, 2)[n]
                with dve.Fori(0, FS - 1) as it:
                    at = segment(f"ffn{n + 1}_loop", it)
                    run(16, {3: [product(norm)], 5: [lambda: h_lo(n, it * 4)]})
                at = segment(f"down{n + 1}")
                run(88, merge({3: [product(norm)], 5: [lambda: h_lo(n, UK * (FS - 1))]},
                              *(x_hooks(norm + 1, s, 22 * (s + 1), 0.5) for s in range(STRIPES - 1))))

            def half_copy(dst):
                nc.vector.tensor_copy(dst, next_fill()[:, SEQ:2 * SEQ]).then_inc(t_dve, 1)

            def t5_rows():
                dve.wait_ge(row_filled, 1)
                nc.vector.tensor_tensor(bias_row[:, :], X1[0:ND, 0:3 * P], lncount[:, :], ALU.add)\
                    .then_inc(row_done, 1)

            def split_fw():
                dve.wait_ge(fw_split, 1)
                nc.vector.tensor_tensor(fw_parts[:, :, NF:2 * NF], fw[:, :, :], fw_parts[:, :, 0:NF].bitcast(F), ALU.subtract)\
                    .then_inc(fw_split, 1)

            def forget_rows():
                dve.wait_ge(f_filled, 1)
                nc.vector.tensor_copy(zT[:, :], X1[0:2 * NF, 0:SEQ]).then_inc(zT_done, 1)

            def forget_gate():
                dve.wait_ge(f_filled, 2)
                step(nc.vector.tensor_copy(z_parts[:, :, :, :], X1[:, 0:2 * TB * NF].rearrange(
                    "p (b n f) -> p b n f", b=TB, n=2)))
                step(nc.vector.tensor_tensor(z_parts[:, :, 0, :], z_parts[:, :, 0, :], z_parts[:, :, 1, :], ALU.add))
                for tb in range(TB):
                    ins = nc.vector.scalar_tensor_tensor(out=fz[:, 0, tb, :], in0=z_parts[:, tb, 0, :],
                                                         scalar=rstd[:, 1, tb:tb + 1], in1=bf[:, :],
                                                         op0=ALU.mult, op1=ALU.add)
                step(ins)
                step(nc.vector.tensor_scalar(fz[:, 5], fz[:, 0], -1.0, None, ALU.mult))
                nc.vector.tensor_tensor(fz[:, 1], fz[:, 0], fz[:, 5], ALU.min).then_inc(f_arg, 1)

            def forget_one():
                dve.wait_ge(f_act, 1)
                nc.vector.tensor_scalar(fz[:, 3], fz[:, 2], 1.0, None, ALU.add).then_inc(f_arg, 1)

            def log_f():
                dve.wait_ge(f_arg, 2)
                step(nc.vector.tensor_scalar(fz[:, 5], fz[:, 3], -1.0, None, ALU.add))
                step(nc.vector.tensor_tensor(fz[:, 5], fz[:, 2], fz[:, 5], ALU.subtract))
                step(nc.vector.reciprocal(fz[:, 1], fz[:, 3]))
                step(nc.vector.tensor_tensor(fz[:, 5], fz[:, 5], fz[:, 1], ALU.mult))
                dve.wait_ge(f_act, 2)
                step(nc.vector.tensor_tensor(fz[:, 5], fz[:, 5], fz[:, 4], ALU.add))
                step(nc.vector.tensor_scalar(fz[:, 0], fz[:, 0], 0.0, None, ALU.min))
                nc.vector.tensor_tensor(fz[:, 0], fz[:, 0], fz[:, 5], ALU.subtract).then_inc(logf_done, 1)

            def mask(a):
                dve.wait_ge(scored, a + 1)
                wait(dve, pT_filled, a - 1)
                S = scores[:, a % 2]
                add = bias[:, a, :] if a < ND else causal
                nc.vector.tensor_tensor_reduce(out=S[:, 0:SEQ], in0=X0[:, 0:SEQ], in1=add, scale=1.0, scalar=2 * NEG,
                                               op0=ALU.add, op1=ALU.max, accum_out=row_max[:, a % 2, 0:1])
                step(nc.vector.tensor_tensor_reduce(out=S[:, SEQ:3 * P], in0=X0[:, SEQ:3 * P], in1=add[:, P:2 * P],
                                                    scale=1.0, scalar=2 * NEG, op0=ALU.add, op1=ALU.max,
                                                    accum_out=row_max[:, a % 2, 1:2]))
                nc.vector.tensor_scalar(neg_max[:, a % 2, :], row_max[:, a % 2, :], -1.0, None, ALU.mult)\
                    .then_inc(masked, 1)

            def normalise(a):
                dve.wait_ge(e_done, a + 1)
                S = scores[:, a % 2]
                step(nc.vector.reciprocal(rdenom[:, a % 2, :], denom[:, a % 2, :]))
                nc.vector.tensor_scalar(S[:, 0:SEQ], S[:, 0:SEQ], rdenom[:, a % 2, 0:1], None, ALU.mult)
                nc.vector.tensor_scalar(S[:, SEQ:3 * P], S[:, SEQ:3 * P], rdenom[:, a % 2, 1:2], None, ALU.mult)\
                    .then_inc(p_done, 1)

            def head_lo(a):
                bank = next_fill()
                head = (a + NF) % NH
                nc.vector.tensor_tensor(oT_lo[:, head, :], bank[:, 0:SEQ], oT_hi[:, head, :].bitcast(F),
                                        ALU.subtract).then_inc(t_dve, 1)

            ffn_rest(0)
            for g in range(4):
                at = segment(f"group{g}")

                def copies(dst):
                    return lambda: [half_copy(dst[:, n, :]) for n in (1, 3)]

                hooks = {17: [copies(qT)], 22: [copies(kT)]}
                if g == 0:
                    hooks = merge(stage_entry(1, 0.5),
                                  {11: [t5_rows, split_fw], 15: [forget_rows], 16: [forget_gate, forget_one], 17: [log_f],
                                   19: [lambda: [half_copy(bias[:, n, :]) for n in (1, 3)]],
                                   23: [lambda: [half_copy(bias[:, n, :]) for n in (5, 7)]]}, hooks)
                else:
                    steps = {}
                    for i in range(GH):
                        a = GH * (g - 1) + i
                        steps.setdefault(4 * i + 3, []).append(lambda a=a: mask(a))
                        steps.setdefault(4 * i + 4, []).append(lambda a=a: normalise(a))
                        steps.setdefault(4 * i + 8, []).append(lambda a=a: head_lo(a))
                    hooks = merge(steps, hooks)
                run(24, hooks)
            at = segment("out")
            steps = {}
            for i in range(GH):
                a = 3 * GH + i
                steps.setdefault(2 * i + 2, []).append(lambda a=a: mask(a))
                steps.setdefault(2 * i + 3, []).append(lambda a=a: normalise(a))
                steps.setdefault(2 * i + 6, []).append(lambda a=a: head_lo(a))
            run(32, merge(steps, *(x_hooks(2, s, OUT_END[s], 1.0, int(s < 2)) for s in range(STRIPES - 1))))
            at = segment("ffn2_first")
            run(16, stage_entry(2, 1.0))
            ffn_rest(1)
            at = segment("ple")

            def embedding_lo():
                bank = next_fill()
                nc.vector.tensor_tensor(pT_lo[:, :, :], bank[:, :].rearrange("p (k t) -> p k t", k=2),
                                        pT_hi[:, :, :].bitcast(F), ALU.subtract).then_inc(t_dve, 1)

            def embed(s):
                def go():
                    dve.wait_ge(mm_done, at("h", 9 * s + 9))
                    cols = slice(s * NW, (s + 1) * NW)
                    for tb in range(TB):
                        dve.wait_ge(drained[0], at.drained(0, s, tb))
                        nc.vector.tensor_tensor(sg[:, tb, :], acc[1][tb][:, :], sg[:, tb, :], ALU.mult)\
                            .then_inc(drained[1], 1)
                        dve.wait_ge(drained[1], at.drained(1, s, tb))
                        nc.vector.tensor_tensor(x_sb[:, tb, cols], x_sb[:, tb, cols], sg[:, tb, :], ALU.add)\
                            .then_inc(x_last, 1)
                return go

            run(36, merge(stage_entry(3, 0.5), {7: [embedding_lo]}, *({9 * s + 12: [embed(s)]} for s in range(STRIPES - 1))),
                PLE_HUS)
            embed(3)()
            mean_square(4)
            inverse_root(4)
            dve.wait_ge(gained, 1)
            for tb in range(TB):
                nc.vector.tensor_scalar(out_sb[:, tb, 0:NW], out_sb[:, tb, 0:NW], rstd[:, 4, tb:tb + 1], None,
                                        ALU.mult).then_inc(out_ready[0], 1)
            cols = slice(3 * NW, D)
            for tb in range(TB):
                nc.vector.scalar_tensor_tensor(out=out_sb[:, tb, cols], in0=x_sb[:, tb, cols],
                                               scalar=rstd[:, 4, tb:tb + 1], in1=gfin[:, cols],
                                               op0=ALU.mult, op1=ALU.mult).then_inc(out_ready[3], 1)


INPUTS = ["x", "p", "norm_ffn1", "ffn1_w_gate", "ffn1_w_up", "ffn1_w_down", "norm_mix", "w_in", "b_f", "w_o",
          "norm_ffn2", "ffn2_w_gate", "ffn2_w_up", "ffn2_w_down", "norm_ple", "w_ple_gate", "w_ple_proj",
          "rel_table", "norm_final"]


def kernel(**inputs):
    import concourse.bacc as bacc
    from concourse.bass_utils import run_bass_kernel_spmd

    nc = bacc.Bacc("TRN2", target_bir_lowering=False, num_devices=1)
    arrays, args = {}, []
    named = [(n, np.ascontiguousarray(inputs[n])) for n in INPUTS]
    named += list(zip(("c_square", "c_onehot", "c_lncount"), shape_constants()))
    for name, a in named:
        arrays[f"in_{name}"] = a
        args.append(nc.dram_tensor(f"in_{name}", a.shape, mybir.dt.from_np(a.dtype), kind="ExternalInput").ap())
    args.append(nc.dram_tensor("out", (1, SEQ, D), mybir.dt.float32, kind="ExternalOutput").ap())
    hybrid_layer(nc, *args)
    r = run_bass_kernel_spmd(nc, [arrays], core_ids=[0])
    return r.results[0]["out"]
```
